# Optimizing a Trainium2 kernel written in Bass

```python
import math
import jax, jax.numpy as jnp
from jax import lax
import numpy as np

D_MODEL = 1024
BATCH = 1
SEQ = 512
DEPTH = 1

CHUNK = 64
CONV_WIDTH = 512
CONV_GROUPS = 8
CONV_TAPS = 3
N_HEADS = 8
HEAD_DIM = 64
ATTN_WIDTH = N_HEADS * HEAD_DIM
D_FF = 4 * D_MODEL
Q_BLOCK = 128
N_MOD = 6
EPS = 1e-6
IN_COLS = 3 * CONV_WIDTH + 3 * ATTN_WIDTH + 2 * D_MODEL


def rms_norm(x, g):
    xf = x.astype(jnp.float32)
    y = xf * lax.rsqrt(jnp.mean(xf * xf, axis=-1, keepdims=True) + EPS)
    return (y * g.astype(jnp.float32)).astype(x.dtype)

def modulate(h, shift, scale):
    return h * (1.0 + scale[:, None, :]) + shift[:, None, :]

def short_conv_branch(b_gate, c_gate, u, conv_w):
    s = u.shape[1]
    v = c_gate * u
    vp = jnp.pad(v, ((0, 0), (CONV_TAPS - 1, 0), (0, 0)))
    y = sum(conv_w[k] * vp[:, k:k + s, :] for k in range(CONV_TAPS))
    return b_gate * y

def stick_breaking_attention(q, k, v):
    b, s, h, dh = q.shape
    qh = jnp.transpose(q, (0, 2, 1, 3))
    kh = jnp.transpose(k, (0, 2, 1, 3))
    vh = jnp.transpose(v, (0, 2, 1, 3))
    inv_sqrt = 1.0 / math.sqrt(dh)
    key_pos = jnp.arange(s)
    n_blocks = s // Q_BLOCK

    def block(i):
        start = i * Q_BLOCK
        q_blk = lax.dynamic_slice_in_dim(qh, start, Q_BLOCK, axis=2)
        z = jnp.einsum('bhqd,bhkd->bhqk', q_blk, kh).astype(jnp.float32) * inv_sqrt
        q_pos = start + jnp.arange(Q_BLOCK)
        mask = key_pos[None, :] < q_pos[:, None]
        log_1m_beta = jnp.where(mask, jax.nn.log_sigmoid(-z), 0.0)
        suffix = lax.cumsum(log_1m_beta, axis=3, reverse=True) - log_1m_beta
        a = jnp.where(mask, jnp.exp(jax.nn.log_sigmoid(z) + suffix), 0.0)
        return jnp.einsum('bhqk,bhkd->bhqd', a, vh.astype(jnp.float32)).astype(q.dtype)

    o = lax.map(block, jnp.arange(n_blocks))
    o = jnp.transpose(o, (1, 0, 3, 2, 4))
    return o.reshape(b, s, h * dh)

def first_inputs(seed: int = 0) -> dict:
    key = jax.random.key(seed)
    ks = jax.random.split(key, 16)
    f32 = jnp.float32
    L, D = DEPTH, D_MODEL

    def nrm(k, shape, fan_in):
        return jax.random.normal(k, shape, f32) * (fan_in ** -0.5)

    def gain(k):
        return 1.0 + 0.05 * jax.random.normal(k, (L, D), f32)

    return {
        "x": jax.random.normal(ks[0], (BATCH, SEQ, D), f32),
        "c": jax.random.normal(ks[1], (BATCH, D), f32),
        "w_ada": nrm(ks[2], (L, D, N_MOD * D), D) * 0.5,
        "b_ada": 0.01 * jax.random.normal(ks[3], (L, N_MOD * D), f32),
        "g_pre_mix": gain(ks[4]),
        "g_post_mix": gain(ks[5]),
        "g_pre_mlp": gain(ks[6]),
        "g_post_mlp": gain(ks[7]),
        "w_in": nrm(ks[8], (L, D, IN_COLS), D),
        "conv_w": nrm(ks[9], (L, CONV_TAPS, CONV_WIDTH), CONV_TAPS),
        "w_proj_conv": nrm(ks[10], (L, CONV_WIDTH, D), CONV_WIDTH),
        "w_proj_attn": nrm(ks[11], (L, ATTN_WIDTH, D), ATTN_WIDTH),
        "w_out": nrm(ks[12], (L, D, D), D),
        "w_mlp_in": nrm(ks[13], (L, D, D_FF), D),
        "w_mlp_out": nrm(ks[14], (L, D_FF, D), D_FF),
    }

def first_block(x, c, w_ada, b_ada, g_pre_mix, g_post_mix, g_pre_mlp, g_post_mlp,
              w_in, conv_w, w_proj_conv, w_proj_attn, w_out, w_mlp_in, w_mlp_out):
    b, s, d = x.shape
    split_pts = np.cumsum([CONV_WIDTH, CONV_WIDTH, CONV_WIDTH,
                           ATTN_WIDTH, ATTN_WIDTH, ATTN_WIDTH, D_MODEL])
    for l in range(DEPTH):
        mod = c @ w_ada[l] + b_ada[l]
        sh1, sc1, gt1, sh2, sc2, gt2 = jnp.split(mod, N_MOD, axis=-1)

        h = modulate(rms_norm(x, g_pre_mix[l]), sh1, sc1)
        proj = h @ w_in[l]
        bg, cg, u, q, k, v, ga, gb = jnp.split(proj, split_pts, axis=-1)
        y_conv = short_conv_branch(bg, cg, u, conv_w[l]) @ w_proj_conv[l]
        o = stick_breaking_attention(q.reshape(b, s, N_HEADS, HEAD_DIM),
                                     k.reshape(b, s, N_HEADS, HEAD_DIM),
                                     v.reshape(b, s, N_HEADS, HEAD_DIM))
        y_attn = o @ w_proj_attn[l]
        merged = jax.nn.sigmoid(ga) * y_conv + jax.nn.sigmoid(gb) * y_attn
        mix_out = merged @ w_out[l]
        x = x + gt1[:, None, :] * rms_norm(mix_out, g_post_mix[l])

        h2 = modulate(rms_norm(x, g_pre_mlp[l]), sh2, sc2)
        ff = jnp.square(jax.nn.relu(h2 @ w_mlp_in[l])) @ w_mlp_out[l]
        x = x + gt2[:, None, :] * rms_norm(ff, g_post_mlp[l])
    return x


GRID_W = 64
N_MEM = 256
D_MIX = D_MODEL
CONV_CH = D_MIX // 2
CONV_K = 31
ATT_HEADS = (D_MIX - CONV_CH) // HEAD_DIM
ATT_KV_HEADS = 2
ATT_WIDTH = ATT_HEADS * HEAD_DIM
KV_WIDTH = ATT_KV_HEADS * HEAD_DIM
IN_COLS_2 = 2 * CONV_CH + ATT_WIDTH + 2 * KV_WIDTH
ROPE_THETA = 10000.0
MEM_HEADS = 4
MEM_HEAD_DIM = D_MODEL // MEM_HEADS
D_FF_2 = 2816
FFN_CONV_K = 3


def rmsnorm(x, g):
    xf = x.astype(jnp.float32)
    y = xf * lax.rsqrt(jnp.mean(xf * xf, axis=-1, keepdims=True) + EPS)
    return (y * g.astype(jnp.float32)).astype(x.dtype)

def layernorm(x, g, b):
    xf = x.astype(jnp.float32)
    mu = jnp.mean(xf, axis=-1, keepdims=True)
    var = jnp.mean(jnp.square(xf - mu), axis=-1, keepdims=True)
    y = (xf - mu) * lax.rsqrt(var + EPS)
    return (y * g.astype(jnp.float32) + b.astype(jnp.float32)).astype(x.dtype)

def dwconv_centred(x, w, b):
    C = x.shape[-1]
    K = w.shape[0]
    pad = (K - 1) // 2
    y = lax.conv_general_dilated(
        x, w[:, None, :].astype(x.dtype), window_strides=(1,), padding=[(pad, pad)],
        dimension_numbers=("NWC", "WIO", "NWC"), feature_group_count=C)
    return y + b.astype(x.dtype)

def axial_rope_tables(S):
    rows = S // GRID_W
    r = jnp.repeat(jnp.arange(rows, dtype=jnp.float32), GRID_W)
    c = jnp.tile(jnp.arange(GRID_W, dtype=jnp.float32), rows)
    axis_dim = HEAD_DIM // 2
    inv = ROPE_THETA ** (-jnp.arange(0, axis_dim, 2, dtype=jnp.float32) / axis_dim)
    ang_r = r[:, None] * inv[None, :]
    ang_c = c[:, None] * inv[None, :]
    return jnp.cos(ang_r), jnp.sin(ang_r), jnp.cos(ang_c), jnp.sin(ang_c)

def rotate_half(x, cos, sin):
    x1, x2 = jnp.split(x, 2, axis=-1)
    return jnp.concatenate([x1 * cos - x2 * sin, x2 * cos + x1 * sin], axis=-1)

def apply_axial_rope(x, tabs):
    cr, sr, cc, sc = tabs
    xf = x.astype(jnp.float32)
    xr, xc = jnp.split(xf, 2, axis=-1)
    out = jnp.concatenate([rotate_half(xr, cr, sr), rotate_half(xc, cc, sc)], axis=-1)
    return out.astype(x.dtype)

def gqa_blocked(q, k, v):
    B, H, S, d = q.shape
    G = H // ATT_KV_HEADS
    nb = S // Q_BLOCK
    qb = q.reshape(B, ATT_KV_HEADS, G, nb, Q_BLOCK, d).transpose(3, 0, 1, 2, 4, 5)
    scale = d ** -0.5

    def one_block(qblk):
        s = jnp.einsum("bkgqd,bksd->bkgqs", qblk, k).astype(jnp.float32) * scale
        p = jax.nn.softmax(s, axis=-1).astype(v.dtype)
        return jnp.einsum("bkgqs,bksd->bkgqd", p, v)

    o = lax.map(one_block, qb)
    return o.transpose(1, 0, 4, 2, 3, 5).reshape(B, S, H * d)

def parallel_mixer(h, w_in, conv_dw, conv_dw_b, conv_ln_g, conv_ln_b, q_norm_g, k_norm_g, w_out, tabs):
    B, S, _ = h.shape
    z = jnp.einsum("bsd,dc->bsc", h, w_in)
    o0 = 2 * CONV_CH
    a_val, a_gate = z[..., :CONV_CH], z[..., CONV_CH:o0]
    q = z[..., o0:o0 + ATT_WIDTH]
    k = z[..., o0 + ATT_WIDTH:o0 + ATT_WIDTH + KV_WIDTH]
    v = z[..., o0 + ATT_WIDTH + KV_WIDTH:]

    a = a_val * jax.nn.sigmoid(a_gate)
    a = dwconv_centred(a, conv_dw, conv_dw_b)
    a = layernorm(a, conv_ln_g, conv_ln_b)
    a = jax.nn.silu(a)

    q = q.reshape(B, S, ATT_HEADS, HEAD_DIM).transpose(0, 2, 1, 3)
    k = k.reshape(B, S, ATT_KV_HEADS, HEAD_DIM).transpose(0, 2, 1, 3)
    v = v.reshape(B, S, ATT_KV_HEADS, HEAD_DIM).transpose(0, 2, 1, 3)
    q = apply_axial_rope(rmsnorm(q, q_norm_g), tabs)
    k = apply_axial_rope(rmsnorm(k, k_norm_g), tabs)
    att = gqa_blocked(q, k, v)

    mixed = jnp.concatenate([a, att], axis=-1)
    return jnp.einsum("bsc,cd->bsd", mixed, w_out)

def memory_cross_attention(h, mem_n, w_mem_q, w_mem_kv, w_mem_o):
    B, S, _ = h.shape
    M = mem_n.shape[1]
    q = jnp.einsum("bsd,de->bse", h, w_mem_q).reshape(B, S, MEM_HEADS, MEM_HEAD_DIM)
    kv = jnp.einsum("bmd,de->bme", mem_n, w_mem_kv)
    k = kv[..., :D_MODEL].reshape(B, M, MEM_HEADS, MEM_HEAD_DIM)
    v = kv[..., D_MODEL:].reshape(B, M, MEM_HEADS, MEM_HEAD_DIM)
    s = jnp.einsum("bshd,bmhd->bhsm", q, k).astype(jnp.float32) * (MEM_HEAD_DIM ** -0.5)
    p = jax.nn.softmax(s, axis=-1).astype(v.dtype)
    o = jnp.einsum("bhsm,bmhd->bshd", p, v).reshape(B, S, D_MODEL)
    return jnp.einsum("bse,ed->bsd", o, w_mem_o)

def conv_gated_ffn(h, w_up, ffn_dw, ffn_dw_b, w_down):
    u = jnp.einsum("bsd,df->bsf", h, w_up)
    u = dwconv_centred(u, ffn_dw, ffn_dw_b)
    gate, val = u[..., :D_FF_2], u[..., D_FF_2:]
    return jnp.einsum("bsf,fd->bsd", jax.nn.gelu(gate, approximate=True) * val, w_down)

def second_inputs(seed: int = 0) -> dict:
    key = jax.random.key(seed)
    ks = iter(jax.random.split(key, 32))
    f32 = jnp.float32

    def nrm(shape, scale):
        return jax.random.normal(next(ks), shape, f32) * scale

    def gain(shape):
        return 1.0 + 0.02 * jax.random.normal(next(ks), shape, f32)

    L = DEPTH
    return {
        "x": jax.random.normal(next(ks), (BATCH, SEQ, D_MODEL), f32),
        "mem": jax.random.normal(next(ks), (BATCH, N_MEM, D_MODEL), f32),
        "norm_mix_pre": gain((L, D_MODEL)),
        "w_in": nrm((L, D_MODEL, IN_COLS_2), D_MODEL ** -0.5),
        "conv_dw": nrm((L, CONV_K, CONV_CH), CONV_K ** -0.5),
        "conv_dw_b": nrm((L, CONV_CH), 0.02),
        "conv_ln_g": gain((L, CONV_CH)),
        "conv_ln_b": nrm((L, CONV_CH), 0.02),
        "q_norm_g": gain((L, HEAD_DIM)),
        "k_norm_g": gain((L, HEAD_DIM)),
        "w_out": nrm((L, D_MIX, D_MODEL), D_MIX ** -0.5),
        "norm_mix_post": gain((L, D_MODEL)),
        "norm_mem_pre": gain((L, D_MODEL)),
        "mem_norm_g": gain((L, D_MODEL)),
        "w_mem_q": nrm((L, D_MODEL, D_MODEL), D_MODEL ** -0.5),
        "w_mem_kv": nrm((L, D_MODEL, 2 * D_MODEL), D_MODEL ** -0.5),
        "w_mem_o": nrm((L, D_MODEL, D_MODEL), D_MODEL ** -0.5),
        "norm_mem_post": gain((L, D_MODEL)),
        "norm_ffn_pre": gain((L, D_MODEL)),
        "w_up": nrm((L, D_MODEL, 2 * D_FF_2), D_MODEL ** -0.5),
        "ffn_dw": nrm((L, FFN_CONV_K, 2 * D_FF_2), FFN_CONV_K ** -0.5),
        "ffn_dw_b": nrm((L, 2 * D_FF_2), 0.02),
        "w_down": nrm((L, D_FF_2, D_MODEL), D_FF_2 ** -0.5),
        "norm_ffn_post": gain((L, D_MODEL)),
    }

def second_block(x, mem, norm_mix_pre, w_in, conv_dw, conv_dw_b, conv_ln_g, conv_ln_b,
              q_norm_g, k_norm_g, w_out, norm_mix_post, norm_mem_pre, mem_norm_g,
              w_mem_q, w_mem_kv, w_mem_o, norm_mem_post, norm_ffn_pre, w_up, ffn_dw,
              ffn_dw_b, w_down, norm_ffn_post):
    S = x.shape[1]
    tabs = axial_rope_tables(S)
    for l in range(DEPTH):
        h = rmsnorm(x, norm_mix_pre[l])
        y = parallel_mixer(h, w_in[l], conv_dw[l], conv_dw_b[l], conv_ln_g[l], conv_ln_b[l],
                           q_norm_g[l], k_norm_g[l], w_out[l], tabs)
        x = x + rmsnorm(y, norm_mix_post[l])
        h = rmsnorm(x, norm_mem_pre[l])
        mem_n = rmsnorm(mem, mem_norm_g[l])
        y = memory_cross_attention(h, mem_n, w_mem_q[l], w_mem_kv[l], w_mem_o[l])
        x = x + rmsnorm(y, norm_mem_post[l])
        h = rmsnorm(x, norm_ffn_pre[l])
        y = conv_gated_ffn(h, w_up[l], ffn_dw[l], ffn_dw_b[l], w_down[l])
        x = x + rmsnorm(y, norm_ffn_post[l])
    return x


def setup_inputs(seed=0):
    out = dict(first_inputs(seed))
    for name, value in second_inputs(seed + 1).items():
        if name != "x":
            out[name + "_2"] = value
    return out


def reference(
    x, c, w_ada, b_ada, g_pre_mix, g_post_mix, g_pre_mlp, g_post_mlp, w_in, conv_w, w_proj_conv,
    w_proj_attn, w_out, w_mlp_in, w_mlp_out, mem_2, norm_mix_pre_2, w_in_2, conv_dw_2,
    conv_dw_b_2, conv_ln_g_2, conv_ln_b_2, q_norm_g_2, k_norm_g_2, w_out_2, norm_mix_post_2,
    norm_mem_pre_2, mem_norm_g_2, w_mem_q_2, w_mem_kv_2, w_mem_o_2, norm_mem_post_2,
    norm_ffn_pre_2, w_up_2, ffn_dw_2, ffn_dw_b_2, w_down_2, norm_ffn_post_2,
):
    x = first_block(
        x, c, w_ada, b_ada, g_pre_mix, g_post_mix, g_pre_mlp, g_post_mlp, w_in, conv_w,
        w_proj_conv, w_proj_attn, w_out, w_mlp_in, w_mlp_out,
    )
    return second_block(
        x, mem_2, norm_mix_pre_2, w_in_2, conv_dw_2, conv_dw_b_2, conv_ln_g_2, conv_ln_b_2,
        q_norm_g_2, k_norm_g_2, w_out_2, norm_mix_post_2, norm_mem_pre_2, mem_norm_g_2,
        w_mem_q_2, w_mem_kv_2, w_mem_o_2, norm_mem_post_2, norm_ffn_pre_2, w_up_2, ffn_dw_2,
        ffn_dw_b_2, w_down_2, norm_ffn_post_2,
    )


_drawn_inputs = setup_inputs


def setup_inputs(seed=0):
    import zlib

    import numpy as np

    out = dict(_drawn_inputs(seed))
    spreads = {}
    factors = {'b_ada': 3.017,
     'norm_mix_pre_2': 3.787,
     'conv_ln_g_2': 3.869,
     'conv_ln_b_2': 4.636,
     'q_norm_g_2': 8.0,
     'k_norm_g_2': 8.0,
     'norm_mix_post_2': 3.833,
     'norm_mem_pre_2': 4.819,
     'mem_norm_g_2': 3.114,
     'norm_mem_post_2': 14.531,
     'norm_ffn_pre_2': 11.34,
     'ffn_dw_b_2': 11.697,
     'norm_ffn_post_2': 24.943,
     'conv_dw_b_2': 3.197}
    for name, (base, spread) in spreads.items():
        noise = np.random.default_rng([zlib.crc32(name.encode()), seed]).standard_normal(out[name].shape)
        drawn = base * np.exp(spread * noise) if base else spread * noise
        out[name] = __import__('jax').numpy.asarray(drawn.astype(out[name].dtype))
    for name, factor in factors.items():
        out[name] = (out[name] * factor).astype(out[name].dtype)
    return out
```

```python
from contextlib import ExitStack, contextmanager
import math

import numpy as np

import concourse.bass as bass
from concourse import mybir

ALU = mybir.AluOpType
ACT = mybir.ActivationFunctionType
AX_X = mybir.AxisListType.X
F32 = mybir.dt.float32
F32R = mybir.dt.float32r

P = 128
T = 512
NT = T // P
D = 1024
DC = D // P
H1, HD = 8, 64
KV2 = 2
NM = 256
MT = NM // P
MH, MHD = 4, 256
CC = 4
K2 = 31
POOL_CC = 1
POOL_TAPS = (4, 4, 4)
EPS = 1e-6
BANKS = 8
SLAB = 2048
SC1 = 1.0 / math.sqrt(HD)
SCM = 1.0 / math.sqrt(MHD)
FF1_Q = 4
FF2 = 2816
FF2_C = FF2 // P
FF2_J = FF2_C // 2

(V_G1, V_GM1, V_CW, V_NMIX, V_NMEM, V_MEMG, V_NFFN, V_CB, V_LNG, V_LNB, V_C, V_BADA) = (
    0, 8, 16, 28, 36, 44, 52, 60, 64, 68, 72, 80)
V_CDW = 128
V_FFN = V_CDW + K2 * CC
V_ALL = V_FFN + 4 * 2 * FF2_C

SLABS = [("w_in", 12), ("pconv", 2), ("gates", 8), ("pattn", 2), ("w_out", 4),
         ("mlp", 8 * FF1_Q), ("w_in2", 7), ("memkv", 8), ("w_out2", 4), ("mem_q", 4), ("mem_o", 4), ("ffn", 3 * FF2_J)]
TILES = [("vec", 1), ("ada01", 2), ("nt1", 8), ("w_in", 24), ("ada25", 6), ("pconv", 8), ("att1", 11 * H1),
         ("pattn", 8), ("w_out", 8), ("nt2", 8), ("mlp", 16 * FF1_Q), ("nt3", 8), ("w_in2a", 8), ("memnt", 4),
         ("w_in2", 8), ("att2", 2 * NT + 2 * 8 + 9 * H1), ("ln", 2), ("w_out2", 8), ("nt4", 8), ("mem_q", 8),
         ("attm", 8 * MH), ("mem_o", 8), ("nt5", 8), ("ffn", 12 * FF2_J)]


def starts(sizes):
    at, out = 0, {}
    for name, n in sizes:
        out[name] = at
        at += n
    return out, at


SLAB0, NSLAB = starts(SLABS)
TILE0, NTILE = starts(TILES)


class Steps:

    def __init__(self, eng, own):
        self.eng, self.own = eng, own
        self.count, self.rounds, self.base, self.last = {}, None, {}, None

    def value(self, sem):
        n = self.count.get(sem.name, 0)
        return self.base[sem.name] + n if sem.name in self.base else n

    def done(self, ins, sem=None, tile=None):
        if tile is not None:
            ins.then_inc(tile.free, 1)
            self.last = (tile.free, tile.use + 1)
            return
        sem = self.own if sem is None else sem
        ins.then_inc(sem, 1)
        self.count[sem.name] = self.count.get(sem.name, 0) + 1
        self.last = (sem, self.value(sem))

    def after(self):
        if self.last is not None:
            self.eng.wait_ge(*self.last)

    @contextmanager
    def loop(self, n, per):
        before = dict(self.count)
        with self.eng.Fori(0, n) as i:
            self.base = {name: i * k + before.get(name, 0) for name, k in per.items()}
            for name in per:
                self.count[name] = 0
            self.last = None
            yield i
            got = {name: self.count[name] for name in per}
            assert got == dict(per), (got, per)
            self.base, self.last = {}, None
        for name, k in per.items():
            self.count[name] = before.get(name, 0) + n * k
        changed = {k for k, v in self.count.items() if v != before.get(k, 0)}
        assert changed <= set(per), changed


def head_order(heads):
    out = [("z", 0)]
    for h in range(heads + 1):
        out += [("z", h + 1)] * (h + 1 < heads) + [("t", h)] * (h < heads) + [("o", h - 1)] * (h >= 1)
    return out


def head_tiles(t0, order, sizes):
    out = {}
    for step in order:
        out[step] = t0
        t0 += sizes[step[0]]
    return out


ATT1_ORDER, ATT2_ORDER, ATTM_ORDER = [], [], head_order(MH)
for _step in head_order(H1):
    if _step[0] == "t":
        ATT1_ORDER.insert(len(ATT1_ORDER) - (_step[1] + 1 < H1), ("g", _step[1]))
    ATT1_ORDER.append(_step)
    ATT2_ORDER.append(_step)
    if _step[0] == "t" and _step[1] < 4:
        ATT2_ORDER.append(("m", 4 + _step[1]))
ATT2_ORDER = [x for m in range(NT) for x in (("m", m), ("r", m))] + ATT2_ORDER
TT = head_tiles(TILE0["att1"], ATT1_ORDER, {"z": NT, "t": NT, "o": 1, "g": 2})
TT2 = head_tiles(TILE0["att2"], ATT2_ORDER, {"z": NT, "t": NT, "o": 1, "r": 2, "m": 2})
TTM = head_tiles(TILE0["attm"], ATTM_ORDER, {"z": NT, "t": MT, "o": 2})
ADA_T = {0: TILE0["ada01"], 1: TILE0["ada01"] + 1, 2: TILE0["ada25"], 3: TILE0["ada25"] + 2,
         4: TILE0["ada25"] + 3, 5: TILE0["ada25"] + 4}
NB = {"nt1": 0, "nt2": NT, "nt3": 2 * NT, "memnt": 3 * NT, "nt4": 3 * NT + MT, "nt5": 4 * NT + MT}


def turned(name, m, h):
    return TILE0[name] + (MT if name == "memnt" else NT) * h + m


def build(nc, A, out):
    with ExitStack() as ctx:
        def sb(name, shape, dt=F32, where=None):
            return (where or ctx).enter_context(nc.sbuf_tensor(name, shape, dt))

        def sem(name):
            return ctx.enter_context(nc.semaphore(name))

        ps = [ctx.enter_context(nc.psum_tensor(f"bank{b}", [P, 512], F32)) for b in range(BANKS)]
        w_raw = sb("w_raw", [P, 2, SLAB])
        w_hi = sb("w_hi", [P, 2, SLAB], F32R)
        w_lo = sb("w_lo", [P, 2, SLAB], F32R)
        x = sb("x", [P, NT, D])
        ident = sb("ident", [P, P])
        ones = sb("ones", [P, P])
        before = sb("before", [P, P])
        not_before = sb("not_before", [P, P])
        vec = sb("vec", [P, V_ALL])
        mod = sb("mod", [P, 4, DC])
        gpost = sb("gpost", [P, 2, D])
        stat = sb("stat", [P, 64])
        smx = sb("smx", [P, 4, 2, NT])
        qks = sb("qks", [P, 3, H1 + KV2])
        eps_t = sb("eps_t", [P, 1])
        with ExitStack() as lend:
            rows = sb("rows", [P, 4, P], where=lend)
        with ExitStack() as lend:
            v1 = sb("v1", [P, NT, T], where=lend)
        with ExitStack() as lend:
            p2b = sb("p2b", [P, NT, T], where=lend)
        xn = sb("xn", [P, 2, D])
        tmp = sb("tmp", [P, 2, 512])
        with ExitStack() as lend:
            p1 = sb("p1", [P, T], where=lend)
        junk = sb("junk", [P, D], mybir.dt.bfloat16)

        W1 = [P * (i + 1) for i in range(NT)]
        O1 = [sum(W1[:i]) + i for i in range(NT)]
        A1 = [sum(W1[::-1][:i]) for i in range(NT + 1)]
        M1W = O1[-1] + W1[-1] + 1
        ht_hi = sb("ht_hi", [P, DC, T], F32R)
        ht_lo = sb("ht_lo", [P, DC, T], F32R)

        ph = ExitStack()
        q1 = sb("q1", [P, CC, T], where=ph)
        k1 = sb("k1", [P, CC, T], where=ph)
        ph2 = ExitStack()
        cv = sb("cv", [P, CC, T], where=ph2)
        cy = sb("cy", [P, CC, T], where=ph2)
        ph2.close()
        mg = sb("mg", [P, DC, T], where=ph)
        yt_hi = sb("yt_hi", [P, CC, T], F32R, where=ph)
        yt_lo = sb("yt_lo", [P, CC, T], F32R, where=ph)
        with ExitStack() as lend:
            ada_w = sb("ada_w", [P, 4, D], where=lend)
            ada_acc = sb("ada_acc", [P, 4, D], where=lend)
            ada_b = sb("ada_b", [P, D], where=lend)
        sgb = sb("sgb", [P, DC, T], where=ph)
        m1 = sb("m1", [P, M1W], where=ph)
        b1 = sb("b1", [P, 2, M1W], where=ph)
        at1 = sb("at1", [P, sum(W1)], where=ph)
        ph.close()

        ph = ExitStack()
        hq_hi = sb("hq_hi", [P, DC, T], F32R, where=ph)
        hq_lo = sb("hq_lo", [P, DC, T], F32R, where=ph)
        hr = sb("hr", [P, 2, T], where=ph)
        facc = sb("facc", [P, NT, D], where=ph)
        ph.close()

        with ExitStack() as lend:
            mem = sb("mem", [P, MT, D], where=lend)
        mem_k = sb("mem_k", [P, DC, NM])
        mem_v = sb("mem_v", [P, MT, D])
        ph = ExitStack()
        mt_hi = sb("mt_hi", [P, DC, NM], F32R, where=ph)
        mt_lo = sb("mt_lo", [P, DC, NM], F32R, where=ph)
        q2 = sb("q2", [P, CC, T], where=ph)
        k2 = sb("k2", [P, KV2, T], where=ph)
        v2 = sb("v2", [P, NT, KV2 * HD], where=ph)
        pad = K2 // 2
        av = sb("av", [P, CC, T + 2 * pad], where=ph)
        ay = sb("ay", [P, CC, T], where=ph)
        with ExitStack() as lend:
            rope = sb("rope", [P, 2, NT, HD], where=lend)
            qkg = sb("qkg", [P, H1 + KV2, HD], where=lend)
            qk = sb("qk", [P, H1 + KV2, HD], where=lend)
            qk_t = sb("qk_t", [P, H1 + KV2, HD], where=lend)
            kd = sb("kd", [P, KV2, 2, HD], where=lend)
            qki = sb("qki", [P, NT, H1 + KV2, HD], where=lend)
        p2a = sb("p2a", [P, NT, T], where=ph)
        pt2 = sb("pt2", [P, NT, T], where=ph)
        lnt = sb("lnt", [P, T], where=ph)
        lnq = sb("lnq", [P, 2, T], where=ph)
        ph.close()

        ph = ExitStack()
        qm = sb("qm", [P, DC, T], where=ph)
        pm = sb("pm", [P, 2, NT, NM], where=ph)
        ptm = sb("ptm", [P, MT, T], where=ph)
        ph.close()

        ph = ExitStack()
        par = sb("par", [P, 2, 8, 2], where=ph)
        uc = sb("uc", [P, 4, T], where=ph)
        gact = sb("gact", [P, 2, T], where=ph)
        hf_hi = sb("hf_hi", [P, 2, 2, T], F32R, where=ph)
        hf_lo = sb("hf_lo", [P, 2, 2, T], F32R, where=ph)
        facc2 = sb("facc2", [P, NT, D], where=ph)
        ph.close()

        psum_full = [sem(f"psum_full{b}") for b in range(BANKS)]
        psum_free = [sem(f"psum_free{b}") for b in range(BANKS)]
        slab_loaded = [sem(f"slab_loaded{r}") for r in range(2)]
        slab_hi, slab_split, slab_free = sem("slab_hi"), sem("slab_split"), sem("slab_free")
        slab_go = sem("slab_go")
        rows_loaded, x_loaded, mem_loaded = sem("rows_loaded"), sem("x_loaded"), sem("mem_loaded")
        ada_b_loaded = [sem(f"ada_b_loaded{i}") for i in range(2)]
        ada_loaded = [sem(f"ada_loaded{r}") for r in range(4)]
        ada_used, gp_made = sem("ada_used"), sem("gp_made")
        tables_loaded, gp_loaded = sem("tables_loaded"), [sem(f"gp_loaded{i}") for i in range(5)]
        consts_made, act_step, dve_step, pool_step = (sem(n) for n in (
            "consts_made", "act_step", "dve_step", "pool_step"))
        norm_std, norm_inv, xn_ready, nt_tmp, nt_hi, nt_lo = (sem(n) for n in (
            "norm_std", "norm_inv", "xn_ready", "nt_tmp", "nt_hi", "nt_lo"))
        post_std, x_new, ffn_scaled, x_added = (sem(n) for n in ("post_std", "x_new", "ffn_scaled", "x_added"))
        part_f32, part_hi, part_lo = sem("part_f32"), sem("part_hi"), sem("part_lo")
        gate_used, o_hi, a1_ready, sm_max, sm_p = (sem(n) for n in ("gate_used", "o_hi", "a1_ready", "sm_max", "sm_p"))
        k_in, rope_ss, rope_std, qk_ready = (sem(n) for n in (
            "k_in", "rope_ss", "rope_std", "qk_ready"))
        ay_pool_ready = sem("ay_pool_ready")
        ay_ready, ln_d, ln_sq, ln_used, ln_y = (sem(n) for n in ("ay_ready", "ln_d", "ln_sq", "ln_used", "ln_y"))
        uc_ready, gact_ready, gu_ready, ffn_hi, ffn_lo = (sem(n) for n in (
            "uc_ready", "gact_ready", "gu_ready", "ffn_hi", "ffn_lo"))
        par_ready, par_go, out_stored = sem("par_ready"), sem("par_go"), sem("out_stored")

        class Tile:

            def __init__(self, t, i=None, per=0):
                assert per % BANKS == 0
                self.b = t % BANKS
                self.use = t // BANKS if i is None else i * (per // BANKS) + t // BANKS
                self.first = i is None and t < BANKS
                self.ap = ps[self.b]

            def wait_free(self, eng):
                if not self.first:
                    eng.wait_ge(psum_free[self.b], self.use)

            def wait_full(self, eng):
                eng.wait_ge(psum_full[self.b], self.use + 1)

            def wait_taken(self, eng):
                eng.wait_ge(psum_free[self.b], self.use + 1)

            @property
            def full(self):
                return psum_full[self.b]

            @property
            def free(self):
                return psum_free[self.b]

        block = ctx.enter_context(nc.Block())
        T0, S0 = TILE0, SLAB0

        def w_rows(w):
            return w.rearrange("(k p) n -> p k n", p=P)

        @block.sync
        def _(sp):
            raw4 = [w_raw[:, r, :].rearrange("p (k n) -> p k n", k=4) for r in range(2)]
            raw2 = [w_raw[:, r, :].rearrange("p (k n) -> p k n", k=2) for r in range(2)]
            raw8 = [w_raw[:, r, :].rearrange("p (k n) -> p k n", k=8) for r in range(2)]
            n = 0

            def load(view, src, at=None):
                nonlocal n
                num = n if at is None else at
                if at is not None or n >= 2:
                    sp.wait_ge(slab_split, num - 1)
                sp.dma_start(view[n % 2], src).then_inc(slab_loaded[n % 2], 16)
                n += 1

            def column_block(w, c0, ks):
                for s in range(ks):
                    load(raw4, w[:, 4 * s:4 * s + 4, c0:c0 + 512])

            wada = A["w_ada"].rearrange("(k p) n -> p k n", p=P)

            def ada(i):
                if i >= 4:
                    sp.wait_ge(ada_used, i - 3)
                s = i // DC
                sp.dma_start(ada_w[:, i % 4], wada[:, i % DC, s * D:(s + 1) * D]).then_inc(ada_loaded[i % 4], 16)

            for i in range(2 * DC):
                ada(i)
            win = w_rows(A["w_in"])
            i = 2 * DC
            for c0 in (512, 1024, 0, 1536, 2048, 2560):
                for s in range(2):
                    load(raw4, win[:, 4 * s:4 * s + 4, c0:c0 + 512])
                    for _ in range(4 if n > 2 else 0):
                        if i < 6 * DC:
                            ada(i)
                            i += 1
            assert i == 6 * DC

            def both_halves(w, order=(0, 1)):
                for s in order:
                    for c0 in (0, 512):
                        load(raw4, w_rows(A[w])[:, 4 * s:4 * s + 4, c0:c0 + 512])

            column_block(w_rows(A["w_proj_conv"]), 0, 1)
            column_block(w_rows(A["w_proj_conv"]), 512, 1)
            for g in range(H1):
                load(raw8, win[:, :, 3072 + 256 * g:3072 + 256 * g + 256])
            for c0 in (0, 512):
                column_block(w_rows(A["w_proj_attn"]), c0, 1)
            both_halves("w_out")
            assert n == S0["mlp"]
            wi, wo = w_rows(A["w_mlp_in"]), w_rows(A["w_mlp_out"])
            n0 = n
            with sp.Fori(0, FF1_Q) as qi:
                n = n0
                for c in range(2):
                    for s in range(2):
                        load(raw4, wi[:, 4 * s:4 * s + 4, bass.ds(qi * 1024 + 512 * c, 512)], qi * 8 + n)
                for s in range(2):
                    for c in range(2):
                        load(raw4, wo[:, bass.ds(qi * 8 + 4 * s, 4), 512 * c:512 * c + 512], qi * 8 + n)
            n = n0 + 8 * FF1_Q
            wi2 = w_rows(A["w_in_2"])
            for c0 in (0, 512, 1024):
                column_block(wi2, c0, 2)
            load(raw8, wi2[:, :, 1536:1792])
            wkv = w_rows(A["w_mem_kv_2"])
            for i in range(8):
                load(raw8, wkv[:, :, 256 * i:256 * i + 256])
            both_halves("w_out_2", (1, 0))
            for c0 in (0, 512):
                column_block(w_rows(A["w_mem_q_2"]), c0, 2)
            both_halves("w_mem_o_2")
            assert n == S0["ffn"] and n % 2 == 1
            wu = w_rows(A["w_up_2"])
            wd = w_rows(A["w_down_2"])

            def up(j, at=None):
                for g in range(2):
                    c0 = j * 256 + g * FF2
                    load(raw8, wu[:, :, c0:c0 + 256] if at is None else wu[:, :, bass.ds(c0, 256)],
                         None if at is None else at + n)

            def down(j, at=None):
                src = wd[:, 2 * j:2 * j + 2, :] if at is None else wd[:, bass.ds(j * 2, 2), :]
                load(raw2, src, None if at is None else at + n)

            up(0)
            n0 = n
            with sp.Fori(0, (FF2_J - 1) // 2) as i:
                n = n0
                up(i * 2 + 1, i * 6)
                down(i * 2, i * 6)
                up(i * 2 + 2, i * 6)
                down(i * 2 + 1, i * 6)
            n = n0 + 6 * ((FF2_J - 1) // 2)
            down(FF2_J - 1)
            assert n == NSLAB
            for m in range(NT):
                sp.wait_ge(*((x_added, m + 1) if m < NT - 1 else (x_new, 4 * NT + 1)))
                sp.dma_start(out[m * P:m * P + P, :], x[:, m, :]).then_inc(out_stored, 16)
            sp.wait_ge(out_stored, 16 * NT)

        @block.gpsimd
        def _(g):
            g.memset(ident[:], 0.0).then_inc(pool_step, 1)
            g.memset(before[:], 1.0).then_inc(pool_step, 1)
            g.memset(not_before[:], 1.0).then_inc(pool_step, 1)
            g.memset(ones[:], 1.0).then_inc(pool_step, 1)
            g.memset(eps_t[:], EPS).then_inc(pool_step, 1)
            g.wait_ge(pool_step, 5)
            g.affine_select(out=ident[:], in_=ident[:], compare_op=ALU.not_equal, fill=1.0, base=0,
                            pattern=[[-1, P]], channel_multiplier=1).then_inc(consts_made, 1)
            g.affine_select(out=before[:], in_=before[:], compare_op=ALU.is_gt, fill=0.0, base=0,
                            pattern=[[-1, P]], channel_multiplier=1).then_inc(consts_made, 1)
            g.affine_select(out=not_before[:], in_=not_before[:], compare_op=ALU.is_ge, fill=0.0, base=0,
                            pattern=[[1, P]], channel_multiplier=-1).then_inc(consts_made, 1)

            def split(n, i=0):
                r = n % 2
                g.wait_ge(slab_loaded[r], i * 16 + 16 * (n // 2 + 1))
                g.wait_ge(slab_free, i * 2 + n + 1)
                g.sem_inc(slab_go, 1)
                g.tensor_scalar(w_hi[:, r], w_raw[:, r], 1.0, 1.0, ALU.mult, ALU.mult).then_inc(slab_hi, 1)
                g.wait_ge(slab_hi, i * 2 + n + 1)
                g.tensor_tensor(w_lo[:, r], w_raw[:, r], w_hi[:, r].bitcast(F32), ALU.subtract).then_inc(slab_split, 1)

            def split_all(a, b):
                with g.Fori(0, (b - a) // 2) as i:
                    split(a, i)
                    split(a + 1, i)
                if (b - a) % 2:
                    split(b - 1)

            st = Steps(g, pool_step)
            st.count[pool_step.name] = 5

            def conv31():
                g.wait_ge(gate_used, DC + CC)
                for c in range(CC - POOL_CC, CC):
                    for k in range(K2):
                        w = vec[:, V_CDW + CC * k + c:V_CDW + CC * k + c + 1]
                        st.after()
                        if k == 0:
                            st.done(g.tensor_scalar(ay[:, c], av[:, c, 0:T], w, vec[:, V_CB + c:V_CB + c + 1], ALU.mult,
                                                    ALU.add))
                        else:
                            st.done(g.tensor_scalar(lnq[:, 0], av[:, c, k:k + T], w, 1.0, ALU.mult, ALU.mult))
                            st.after()
                            st.done(g.tensor_tensor(ay[:, c], ay[:, c], lnq[:, 0], ALU.add),
                                    ay_pool_ready if k == K2 - 1 else None)
                        yield

            taps = conv31()
            n = S0["memkv"] + 6
            split_all(0, n)
            for k in POOL_TAPS:
                for _ in range(k):
                    next(taps, None)
                split(n)
                n += 1
            for _ in taps:
                pass
            split_all(n, NSLAB)
            for m in range(NT - 1):
                g.wait_ge(ffn_scaled, m + 1)
                g.tensor_tensor(x[:, m], x[:, m], facc2[:, m], ALU.add).then_inc(x_added, 1)

        @block.tensor
        def _(pe):
            state = {"slab": 0, "owed": True}

            def inc_free(ins):
                if state["owed"]:
                    ins.then_inc(slab_free, 1)
                    state["owed"] = False
                return ins

            def slab(i=None, per=0):
                n = state["slab"]
                state["slab"] += 1
                pe.wait_ge(slab_split, n + 1 if i is None else i * per + n + 1)
                return n % 2

            def mm3(o, ah, al, bh, bl, start, stop):
                inc_free(pe.matmul(o, ah, bh, start=start, stop=False))
                pe.matmul(o, al, bh, start=False, stop=False)
                return pe.matmul(o, ah, bl, start=False, stop=stop)

            def wv(r, k):
                return (w_hi[:, r].rearrange("p (k n) -> p k n", k=k), w_lo[:, r].rearrange("p (k n) -> p k n", k=k))

            def all_taken(ts):
                for t in ts:
                    Tile(t).wait_taken(pe)

            def features(t0, ks, ah, al, i=None, tper=0, sper=0, n=T, rows=None):
                for s in range(ks):
                    r = slab(i, sper)
                    wh, wl = wv(r, 4)
                    if s == 1 and rows is not None:
                        pe.wait_ge(nt_lo, 2 * (NB[rows] + NT))
                    for m in range(4):
                        t = Tile(t0 + m, i, tper)
                        if s == 0:
                            t.wait_free(pe)
                        for k in range(4):
                            c = slice(m * P, m * P + P)
                            ins = mm3(t.ap[:, 0:n], wh[:, k, c], wl[:, k, c], ah[:, 4 * s + k], al[:, 4 * s + k],
                                      s == 0 and k == 0, s == ks - 1 and k == 3)
                        if s == ks - 1:
                            ins.then_inc(t.full, 1)
                    state["owed"] = True

            def tokens(t0, ks, ah, al, i=None, tper=0, sper=0):
                for s in range(ks):
                    r = slab(i, sper)
                    tokens_slab(t0, r, s, s == 0, s == ks - 1, ah, al, i, tper)

            def tokens_tile(t, wh, wl, s, m, start, stop, ah, al):
                if start:
                    t.wait_free(pe)
                for k in range(4):
                    c = slice(m * P, m * P + P)
                    ins = mm3(t.ap[:], ah[:, 4 * s + k, c], al[:, 4 * s + k, c], wh[:, k], wl[:, k],
                              start and k == 0, stop and k == 3)
                if stop:
                    ins.then_inc(t.full, 1)

            def tokens_slab(t0, r, s, start, stop, ah, al, i=None, tper=0):
                wh, wl = wv(r, 4)
                for m in range(NT):
                    tokens_tile(Tile(t0 + m, i, tper), wh, wl, s, m, start, stop, ah, al)
                state["owed"] = True

            def rows_of_1024(t0, ready, ah, al, i=None, tper=0, sper=0, order=(0, 1), by_rows=True):
                for s in order:
                    ready(s)
                    if by_rows and s == order[1]:
                        w = {}
                        for h, m in ((0, 0), (0, 1), (0, 2), (1, 0), (1, 1), (0, 3), (1, 2), (1, 3)):
                            if h not in w:
                                w[h] = wv(slab(i, sper), 4)
                            tokens_tile(Tile(t0 + 4 * h + m, i, tper), *w[h], s, m, False, True, ah, al)
                            if m == NT - 1:
                                state["owed"] = True
                    else:
                        for h in range(2):
                            tokens_slab(t0 + 4 * h, slab(i, sper), s, s == order[0], s == order[1], ah, al, i, tper)

            def narrow(t0, ah, al, stand, i=None, tper=0, sper=0, n=T):
                wh, wl = wv(slab(i, sper), DC)
                for m in range(2):
                    t = Tile(t0 + m, i, tper)
                    t.wait_free(pe)
                    for k in range(DC):
                        c = slice(m * P, m * P + P)
                        a = (wh[:, k, c], wl[:, k, c], ah[:, k], al[:, k]) if stand else (
                            ah[:, k, c], al[:, k, c], wh[:, k], wl[:, k])
                        ins = mm3(t.ap[:, 0:n], *a, k == 0, k == DC - 1)
                    ins.then_inc(t.full, 1)
                state["owed"] = True

            def transposes(name):
                for m in range(MT if name == "memnt" else NT):
                    pe.wait_ge(xn_ready, NB[name] + m + 1)
                    for h in range(2):
                        t = Tile(turned(name, m, h))
                        t.wait_free(pe)
                        for c in range(4):
                            ins = pe.transpose(t.ap[:, c * P:c * P + P], xn[:, m % 2, (4 * h + c) * P:(4 * h + c + 1) * P],
                                               ident[:])
                        ins.then_inc(t.full, 1)

            pe.sem_inc(slab_free, 1)
            pe.wait_ge(consts_made, 3)
            pe.wait_ge(rows_loaded, 16 * 16)
            t = Tile(T0["vec"])
            at = 0
            for j, n in enumerate((P, K2 * CC, 88, 88)):
                ins = pe.transpose(t.ap[:, at:at + n], rows[0:n, j, :], ident[0:n, 0:n])
                at += n
            ins.then_inc(t.full, 1)
            def modulation(s):
                pe.wait_ge(ada_used, DC * (s + 1))
                acc = ada_acc[:, s % 4]
                for h in range(2 if s in (2, 5) else 1):
                    t = Tile(ADA_T[s] + h)
                    t.wait_free(pe)
                    if s in (2, 5):
                        ins = pe.matmul(t.ap[:], ones[:], acc[:, 512 * h:512 * h + 512], start=True, stop=True)
                    else:
                        for c in range(DC):
                            ins = pe.matmul(t.ap[:, c:c + 1], acc[:, c * P:c * P + P], ones[:, 0:1],
                                            start=True, stop=True)
                    ins.then_inc(t.full, 1)

            modulation(0)
            modulation(1)

            def split_rows(name):
                pe.wait_ge(nt_lo, 2 * (NB[name] + MT) if name == "memnt" else 2 * (NB[name] + NT) - 1)

            transposes("nt1")
            split_rows("nt1")
            with pe.Fori(0, 2) as i:
                for c in range(2):
                    features(T0["w_in"] + 4 * c, 2, ht_hi, ht_lo, i, 8, 4, rows="nt1")
            state["slab"] += 4
            features(T0["w_in"] + 16, 2, ht_hi, ht_lo)
            tokens(T0["w_in"] + 20, 2, ht_hi, ht_lo)
            for s in range(2, 6):
                modulation(s)
            pe.wait_ge(part_lo, CC)
            for c in range(2):
                features(T0["pconv"] + 4 * c, 1, yt_hi, yt_lo)
            def scores1(h):
                o, c = HD * (h % 2), h // 2
                for qt in range(NT):
                    t = Tile(TT["z", h] + qt)
                    t.wait_free(pe)
                    ins = pe.matmul(t.ap[:, 0:W1[qt]], q1[o:o + HD, c, qt * P:qt * P + P], k1[o:o + HD, c, 0:W1[qt]],
                                    start=True, stop=True)
                    ins.then_inc(t.full, 1)

            def turn1(h):
                for kc in range(NT):
                    t = Tile(TT["t", h] + kc)
                    t.wait_free(pe)
                    if kc == 0:
                        pe.wait_ge(a1_ready, NT * (h + 1))
                    for qt in range(kc, NT):
                        ins = pe.transpose(t.ap[:, qt * P:qt * P + P], b1[:, h % 2, O1[qt] + kc * P:O1[qt] + kc * P + P],
                                           ident[:])
                    ins.then_inc(t.full, 1)

            def values1(h):
                o = HD * (h % 2)
                t = Tile(TT["o", h])
                t.wait_free(pe)
                all_taken(range(TT["t", h], TT["t", h] + NT))
                for kc in range(NT):
                    ins = pe.matmul(t.ap[o:o + HD, kc * P:T], v1[:, kc, h * HD:h * HD + HD], at1[:, A1[kc]:A1[kc + 1]],
                                    start=kc == 0, stop=kc == NT - 1)
                ins.then_inc(t.full, 1)

            all_taken(range(T0["w_in"] + 12, T0["w_in"] + 24))
            for what, h in ATT1_ORDER:
                if what == "g":
                    narrow(TT[what, h], ht_hi, ht_lo, True)
                else:
                    {"z": scores1, "t": turn1, "o": values1}[what](h)
            all_taken(TT["o", h] for h in range(H1))
            for c in range(2):
                features(T0["pattn"] + 4 * c, 1, yt_hi, yt_lo)
            rows_of_1024(T0["w_out"], lambda s: pe.wait_ge(part_lo, CC + 4 * s + 4), ht_hi, ht_lo)
            transposes("nt2")
            split_rows("nt2")
            def mlp_quarter(q, t0, i=None):
                tper, sper = 16, 8
                for c in range(2):
                    features(t0 + 4 * c, 2, ht_hi, ht_lo, i, tper, sper, rows="nt2")
                rows_of_1024(t0 + 8, lambda s: pe.wait_ge(part_lo, q * DC + CC + DC + 4 * s + 4), hq_hi, hq_lo,
                             i, tper, sper, by_rows=i is None)

            with pe.Fori(0, FF1_Q - 1) as i:
                mlp_quarter(i, T0["mlp"], i)
            state["slab"] += 8 * (FF1_Q - 2)
            mlp_quarter(FF1_Q - 1, T0["mlp"] + 16 * (FF1_Q - 1))
            transposes("nt3")
            split_rows("nt3")
            for c in range(2):
                features(T0["w_in2a"] + 4 * c, 2, ht_hi, ht_lo, rows="nt3")
            transposes("memnt")
            tokens(T0["w_in2"], 2, ht_hi, ht_lo)
            wh, wl = wv(slab(), DC)
            for m in range(NT):
                t = Tile(T0["w_in2"] + 4 + m)
                t.wait_free(pe)
                for k in range(DC):
                    c = slice(m * P, m * P + P)
                    ins = mm3(t.ap[:, 0:256], ht_hi[:, k, c], ht_lo[:, k, c], wh[:, k], wl[:, k], k == 0, k == DC - 1)
                ins.then_inc(t.full, 1)
            state["owed"] = True
            split_rows("memnt")

            def turn_qk(m):
                pe.wait_ge(qk_ready, m + 1)
                t = Tile(TT2["r", m])
                t.wait_free(pe)
                for c in range(CC):
                    ins = pe.transpose(t.ap[:, c * P:c * P + P], qk[:, 2 * c:2 * c + 2, :].rearrange("p a d -> p (a d)"),
                                       ident[:])
                ins.then_inc(t.full, 1)
                t = Tile(TT2["r", m] + 1)
                t.wait_free(pe)
                for g in range(KV2):
                    ins = pe.transpose(t.ap[:, g * P:g * P + P], kd[:, g].rearrange("p a d -> p (a d)"), ident[:])
                ins.then_inc(t.full, 1)

            def memory_kv(j):
                narrow(TT2["m", j], mt_hi, mt_lo, j < 4, n=NM)

            def scores2(h):
                o, c = HD * (h % 2), h // 2
                for qt in range(NT):
                    t = Tile(TT2["z", h] + qt)
                    t.wait_free(pe)
                    pe.matmul(t.ap[:], q2[o:o + HD, c, qt * P:qt * P + P], k2[o:o + HD, h // 4, :],
                              start=True, stop=True).then_inc(t.full, 1)

            def turn2(h):
                pe.wait_ge(sm_p, NT * (h + 1))
                for kc in range(NT):
                    t = Tile(TT2["t", h] + kc)
                    t.wait_free(pe)
                    for qt in range(NT):
                        ins = pe.transpose(t.ap[:, qt * P:qt * P + P], (p2a, p2b)[h % 2][:, qt, kc * P:kc * P + P], ident[:])
                    ins.then_inc(t.full, 1)

            def values2(h):
                o = HD * (h % 2)
                t = Tile(TT2["o", h])
                t.wait_free(pe)
                all_taken(range(TT2["t", h], TT2["t", h] + NT))
                for kc in range(NT):
                    ins = pe.matmul(t.ap[o:o + HD, :], v2[:, kc, (h // 4) * HD:(h // 4) * HD + HD], pt2[:, kc],
                                    start=kc == 0, stop=kc == NT - 1)
                ins.then_inc(t.full, 1)

            for what, h in ATT2_ORDER:
                if (what, h) == ("z", 0):
                    all_taken(TT2["r", m] + c for m in range(NT) for c in range(2))
                    all_taken(range(T0["w_in2"] + 4, T0["w_in2"] + 8))
                {"z": scores2, "t": turn2, "o": values2, "r": turn_qk, "m": memory_kv}[what](h)
            t = Tile(T0["ln"])
            t.wait_free(pe)
            pe.wait_ge(ay_ready, CC - POOL_CC)
            pe.wait_ge(ay_pool_ready, POOL_CC)
            for c in range(CC):
                ins = pe.matmul(t.ap[:], ones[:], ay[:, c], start=c == 0, stop=c == CC - 1)
            ins.then_inc(t.full, 1)
            t = Tile(T0["ln"] + 1)
            t.wait_free(pe)
            for c in range(CC):
                pe.wait_ge(ln_sq, c + 1)
                ins = pe.matmul(t.ap[:], ones[:], lnq[:, c % 2], start=c == 0, stop=c == CC - 1)
                if c < CC - 1:
                    ins.then_inc(ln_used, 1)
            ins.then_inc(t.full, 1)

            def mixed_ready(s):
                if s:
                    all_taken(TT2["o", h] for h in range(H1))
                else:
                    pe.wait_ge(part_lo, CC + DC + DC * FF1_Q + CC)

            rows_of_1024(T0["w_out2"], mixed_ready, ht_hi, ht_lo, order=(1, 0))
            transposes("nt4")
            split_rows("nt4")
            for c in range(2):
                features(T0["mem_q"] + 4 * c, 2, ht_hi, ht_lo, rows="nt4")

            def scoresm(h):
                for qt in range(NT):
                    t = Tile(TTM["z", h] + qt)
                    t.wait_free(pe)
                    for c in range(2):
                        ins = pe.matmul(t.ap[:, 0:NM], qm[:, 2 * h + c, qt * P:qt * P + P], mem_k[:, 2 * h + c, :],
                                        start=c == 0, stop=c == 1)
                    ins.then_inc(t.full, 1)

            def turnm(h):
                pe.wait_ge(sm_p, NT * (H1 + h + 1))
                for kc in range(MT):
                    t = Tile(TTM["t", h] + kc)
                    t.wait_free(pe)
                    for qt in range(NT):
                        ins = pe.transpose(t.ap[:, qt * P:qt * P + P], pm[:, h % 2, qt, kc * P:kc * P + P], ident[:])
                    ins.then_inc(t.full, 1)

            def valuesm(h):
                all_taken(range(TTM["t", h], TTM["t", h] + MT))
                for c in range(2):
                    t = Tile(TTM["o", h] + c)
                    t.wait_free(pe)
                    for kc in range(MT):
                        ins = pe.matmul(t.ap[:], mem_v[:, kc, h * MHD + c * P:h * MHD + c * P + P], ptm[:, kc],
                                        start=kc == 0, stop=kc == MT - 1)
                    ins.then_inc(t.full, 1)

            all_taken(range(T0["mem_q"], T0["mem_q"] + DC))
            for what, h in ATTM_ORDER:
                {"z": scoresm, "t": turnm, "o": valuesm}[what](h)
            rows_of_1024(T0["mem_o"], lambda s: all_taken(TTM["o", 2 * s + h] + c for h in range(2) for c in range(2)),
                         ht_hi, ht_lo)
            transposes("nt5")
            pe.wait_ge(nt_lo, 2 * (NB["nt5"] + NT))

            def ffn_up(t0, i=None):
                for s in range(2):
                    narrow(t0 + 2 * s, ht_hi, ht_lo, True, i, 24, 6)

            def ffn_down(t0, j, p, i=None):
                r = slab(i, 6)
                wh, wl = wv(r, 2)
                pe.wait_ge(ffn_lo, j * 2 + 2)
                for m in range(NT):
                    for h in range(2):
                        t = Tile(t0 + 2 * m + h, i, 24)
                        t.wait_free(pe)
                        for k in range(2):
                            c = slice(m * P, m * P + P)
                            hc = slice(512 * h, 512 * h + 512)
                            ins = mm3(t.ap[:], hf_hi[:, p, k, c], hf_lo[:, p, k, c], wh[:, k, hc], wl[:, k, hc],
                                      k == 0, k == 1)
                        ins.then_inc(t.full, 1)
                state["owed"] = True

            t0 = T0["ffn"]
            ffn_up(t0)
            with pe.Fori(0, (FF2_J - 1) // 2) as i:
                ffn_up(t0 + 4, i)
                ffn_down(t0 + 8, i * 2, 0, i)
                ffn_up(t0 + 16, i)
                ffn_down(t0 + 20, i * 2 + 1, 1, i)
            rounds = (FF2_J - 1) // 2
            state["slab"] += 6 * (rounds - 1)
            ffn_down(t0 + 4 + 24 * rounds, FF2_J - 1, 0)
            assert state["slab"] == NSLAB

        @block.scalar
        def _(act):
            st = Steps(act, act_step)

            at = 0
            for name in ("g_pre_mix", "g_pre_mlp", "conv_w", "norm_mix_pre_2", "norm_mem_pre_2", "mem_norm_g_2",
                         "norm_ffn_pre_2", "conv_dw_b_2", "conv_ln_g_2", "conv_ln_b_2", "c", "b_ada"):
                v = A[name].rearrange("(r p) -> r p", p=P)
                act.dma_start(rows[at:at + v.shape[0], 0, :], v).then_inc(rows_loaded, 16)
                at += v.shape[0]
            assert at == P
            act.dma_start(rows[0:K2 * CC, 1, :], A["conv_dw_2"].rearrange("(r p) -> r p", p=P)).then_inc(rows_loaded, 16)
            fd = A["ffn_dw_2"].rearrange("(r p) -> r p", p=P)
            act.dma_start(rows[0:88, 2, :], fd[0:88]).then_inc(rows_loaded, 16)
            act.dma_start(rows[0:44, 3, :], fd[88:132]).then_inc(rows_loaded, 16)
            act.dma_start(rows[44:88, 3, :], A["ffn_dw_b_2"].rearrange("(r p) -> r p", p=P)).then_inc(rows_loaded, 16)
            act.dma_start(x[:], A["x"].rearrange("(m p) d -> p m d", p=P)).then_inc(x_loaded, 16)

            def load_ada_b(j, s):
                act.dma_start(ada_b[:], A["b_ada"][s * D:(s + 1) * D].partition_broadcast(P)).then_inc(ada_b_loaded[j], 16)

            load_ada_b(0, 2)
            for j, name in enumerate(("g_post_mix", "g_post_mlp")):
                act.dma_start(gpost[:, j], A[name].partition_broadcast(P)).then_inc(gp_loaded[j], 16)

            def norm_stat(name, m, src):
                st.after()
                st.done(act.activation(junk[:], src, ACT.Square, accum_out=stat[:, m:m + 1]))
                st.after()
                st.done(act.activation(stat[:, 8 + m:9 + m], stat[:, m:m + 1], ACT.Sqrt, bias=eps_t[:, 0:1],
                                       scale=1.0 / D), norm_std)

            def norm_row(name, m, src):
                act.wait_ge(norm_inv, NB[name] + m + 1)
                if m >= 2:
                    Tile(turned(name, m - 2, 1)).wait_full(act)
                st.done(act.activation(xn[:, m % 2], src, ACT.Copy, scale=stat[:, 16 + m:17 + m]), xn_ready)

            def norm(name, m, src):
                norm_stat(name, m, src)
                norm_row(name, m, src)

            def norm_hi(name, m, hi, shifted=None, halves=(0, 1)):
                for h in halves:
                    if shifted is None:
                        Tile(turned(name, m, h)).wait_taken(act)
                    else:
                        act.wait_ge(nt_tmp, 2 * (NT * shifted + m) + h + 1)
                    st.done(act.copy(hi[:, 4 * h:4 * h + 4, m * P:m * P + P],
                                     tmp[:, h].rearrange("p (c t) -> p c t", c=4)), nt_hi)

            def post_psum(m, t0):
                for h in range(2):
                    Tile(t0 + 4 * h + m).wait_full(act)
                    st.after()
                    st.done(act.activation(junk[:, 0:512], Tile(t0 + 4 * h + m).ap[:], ACT.Square,
                                           scale=1.0 / math.sqrt(D), accum_out=stat[:, 24 + 8 * h + m:25 + 8 * h + m]))
                    st.after()
                    if h == 0:
                        st.done(act.activation(stat[:, 40 + m:41 + m], stat[:, 24 + m:25 + m], ACT.Identity,
                                               bias=eps_t[:, 0:1]))
                    else:
                        st.done(act.activation(stat[:, 48 + m:49 + m], stat[:, 32 + m:33 + m], ACT.Sqrt,
                                               bias=stat[:, 40 + m:41 + m]), post_std)

            def post_sbuf(src, m, last):
                for t in last:
                    Tile(t).wait_taken(act)
                st.after()
                st.done(act.activation(junk[:], src[:, m], ACT.Square, accum_out=stat[:, 24 + m:25 + m]))
                st.after()
                st.done(act.activation(stat[:, 48 + m:49 + m], stat[:, 24 + m:25 + m], ACT.Sqrt,
                                       bias=eps_t[:, 0:1], scale=1.0 / D), post_std)

            def post_and_norm(u, post, name, hi, shifted=None):
                post(0)
                for m in range(NT + 1):
                    if m + 1 < NT:
                        post(m + 1)
                    if m < NT:
                        act.wait_ge(x_new, NT * u + m + 1)
                        norm_stat(name, m, x[:, m])
                    if m:
                        norm_hi(name, m - 1, hi, shifted, (0,))
                    if m < NT:
                        norm_row(name, m, x[:, m])
                    if m:
                        norm_hi(name, m - 1, hi, shifted, (1,))
                if u + 2 < 5:
                    name = ("norm_mix_post_2", "norm_mem_post_2", "norm_ffn_post_2")[u]
                    act.dma_start(gpost[:, u % 2], A[name].partition_broadcast(P)).then_inc(gp_loaded[u + 2], 16)

            def copy_out(t, dst, n=T):
                t = Tile(t)
                t.wait_full(act)
                st.done(act.copy(dst, t.ap[:, 0:n]), tile=t)

            act.wait_ge(consts_made, 3)
            act.wait_ge(x_loaded, 16)
            for m in range(NT + 1):
                if m < NT:
                    norm("nt1", m, x[:, m])
                if m:
                    norm_hi("nt1", m - 1, ht_hi, 0)
            t0 = T0["w_in"]
            for m in range(CC):
                copy_out(t0 + m, cv[:, m])
            for m in range(CC):
                Tile(t0 + 8 + m).wait_taken(act)
                st.done(act.copy(yt_hi[:, m], cy[:, m]), part_hi)
            for m in range(CC):
                copy_out(t0 + 12 + m, q1[:, m])
            for m in range(CC):
                copy_out(t0 + 16 + m, k1[:, m])
            for m in range(NT):
                copy_out(t0 + 20 + m, v1[:, m])
            act.wait_ge(gp_made, 2)
            load_ada_b(1, 5)
            for m in range(DC):
                copy_out(T0["pconv"] + m, mg[:, m])
            def split_head(t, dst, h, n):
                t = Tile(t)
                t.wait_full(act)
                p0, p1_ = (0, P) if h is None else (HD * (h % 2), HD * (h % 2) + HD)
                st.done(act.copy(dst[p0:p1_, n], t.ap[p0:p1_, :]), o_hi)

            for what, h in ATT1_ORDER:
                if what == "g":
                    for j in range(2):
                        n = 2 * h + j
                        t = Tile(TT["g", h] + j)
                        t.wait_full(act)
                        if n == 0:
                            act.wait_ge(gp_made, 4)
                        if 2 <= n < DC:
                            act.wait_ge(gate_used, n - 1)
                        st.done(act.activation(tmp[:, n % 2] if n < DC else sgb[:, n - DC], t.ap[:], ACT.Sigmoid),
                                tile=t)
                elif what == "z":
                    for qt in range(NT):
                        t = Tile(TT["z", h] + qt)
                        w = W1[qt]
                        t.wait_full(act)
                        if h >= 1:
                            act.wait_ge(a1_ready, NT * (h - 1) + qt + 1)
                        if h >= 2 and qt == 0:
                            Tile(TT["t", h - 2] + NT - 1).wait_full(act)
                        st.done(act.activation(m1[:, O1[qt]:O1[qt] + w], t.ap[:, 0:w], ACT.Sigmoid, scale=-SC1))
                        st.done(act.activation(b1[:, h % 2, O1[qt]:O1[qt] + w], t.ap[:, 0:w], ACT.Sigmoid, scale=SC1),
                                tile=t)
                elif what == "t":
                    for kc in range(NT):
                        t = Tile(TT["t", h] + kc)
                        t.wait_full(act)
                        if h >= 1 and kc == 0:
                            Tile(TT["o", h - 1]).wait_full(act)
                        st.done(act.copy(at1[:, A1[kc]:A1[kc + 1]], t.ap[:, kc * P:T]), tile=t)
                else:
                    split_head(TT["o", h], yt_hi, h, h // 2)
            for m in range(DC):
                act.wait_ge(part_f32, m + 1)
                st.done(act.copy(ht_hi[:, m], mg[:, m]), part_hi)
            post_and_norm(0, lambda m: post_psum(m, T0["w_out"]), "nt2", ht_hi, 1)

            def relu_quarter(q, t0, i=None):
                for m in range(DC + 1):
                    if m < DC:
                        t = Tile(t0 + m, i, 16)
                        t.wait_full(act)
                        st.done(act.activation(hr[:, m % 2], t.ap[:], ACT.Relu), tile=t)
                    if m:
                        act.wait_ge(part_f32, q * DC + DC + m)
                        st.done(act.copy(hq_hi[:, m - 1], tmp[:, (m - 1) % 2]), part_hi)

            with st.loop(FF1_Q - 1, {"part_hi": DC}) as i:
                relu_quarter(i, T0["mlp"], i)
            relu_quarter(FF1_Q - 1, T0["mlp"] + 16 * (FF1_Q - 1))
            last = T0["mlp"] + 16 * (FF1_Q - 1) + 8
            post_and_norm(1, lambda m: post_sbuf(facc, m, (last + m, last + 4 + m)), "nt3", ht_hi)
            act.dma_start(rope[:, 0], A["rope_cos"].rearrange("(m p) d -> p m d", p=P)).then_inc(tables_loaded, 16)
            act.dma_start(rope[:, 1], A["rope_sin"].rearrange("(m p) d -> p m d", p=P)).then_inc(tables_loaded, 16)
            for h in range(H1 + KV2):
                act.dma_start(qkg[:, h], A["q_norm_g_2" if h < H1 else "k_norm_g_2"].partition_broadcast(P)).then_inc(
                    tables_loaded, 16)
            act.dma_start(mem[:], A["mem_2"].rearrange("(m p) d -> p m d", p=P)).then_inc(mem_loaded, 16)
            act.wait_ge(mem_loaded, 16)
            for m in range(MT):
                norm("memnt", m, mem[:, m])
            t0 = T0["w_in2a"]
            for m in range(CC):
                copy_out(t0 + m, av[:, m, pad:pad + T])
            for m in range(CC):
                t = Tile(t0 + 4 + m)
                t.wait_full(act)
                act.wait_ge(gate_used, DC + m - 1)
                st.done(act.activation(tmp[:, m % 2], t.ap[:], ACT.Sigmoid), tile=t)
            for m in range(MT):
                norm_hi("memnt", m, mt_hi)
            t0 = T0["w_in2"]
            for m in range(NT):
                t = Tile(t0 + m)
                t.wait_full(act)
                st.done(act.copy(qki[:, m, 0:H1].rearrange("p h d -> p (h d)"), t.ap[:]), tile=t)
            for m in range(NT):
                t = Tile(t0 + 4 + m)
                t.wait_full(act)
                st.done(act.copy(qki[:, m, H1:].rearrange("p h d -> p (h d)"), t.ap[:, 0:KV2 * HD]), k_in)
                st.done(act.copy(v2[:, m], t.ap[:, KV2 * HD:2 * KV2 * HD]), tile=t)

            def qk_out(m):
                if m < NT:
                    act.wait_ge(rope_ss, m + 1)
                    st.done(act.activation(qks[:, 1], qks[:, 0], ACT.Sqrt, bias=eps_t[:, 0:1], scale=1.0 / HD), rope_std)

            def other(what, j):
                if what == "m":
                    for c in range(2):
                        t = Tile(TT2["m", j] + c)
                        t.wait_full(act)
                        dst = mem_k[:, 2 * j + c] if j < 4 else mem_v[:, c, 256 * (j - 4):256 * (j - 4) + 256]
                        st.done(act.copy(dst, t.ap[:, 0:NM]), tile=t)
                elif what == "r":
                    for n, dst in enumerate((q2, k2)):
                        t = Tile(TT2["r", j] + n)
                        t.wait_full(act)
                        nc_ = dst.shape[1]
                        st.done(act.copy(dst[:, :, j * P:j * P + P],
                                         t.ap[:, 0:nc_ * P].rearrange("p (c t) -> p c t", c=nc_)), tile=t)
                    if j + 1 < NT:
                        qk_out(j + 1)

            qk_out(0)

            def softmax_attention(order, tt, heads, keys, p_of, pt, scale, mb, out_of):
                for what, h in order:
                    if what == "z":
                        for qt in range(NT):
                            t = Tile(tt["z", h] + qt)
                            act.wait_ge(sm_max, mb + NT * h + qt + 1)
                            if h >= 2 and qt == 0:
                                Tile(tt["t", h - 2] + keys // P - 1).wait_full(act)
                            st.done(act.activation(p_of(h)[:, qt], t.ap[:, 0:keys], ACT.Exp, scale=scale,
                                                   bias=smx[:, 0, h % 2, qt:qt + 1],
                                                   accum_out=smx[:, 1, h % 2, qt:qt + 1]), tile=t)
                    elif what == "t":
                        for kc in range(keys // P):
                            t = Tile(tt["t", h] + kc)
                            t.wait_full(act)
                            if h >= 1 and kc == 0:
                                Tile(tt["o", h - 1] + len(out_of(h)) - 1).wait_full(act)
                            st.done(act.copy(pt[:, kc], t.ap[:]), tile=t)
                    elif what in "mr":
                        other(what, h)
                    else:
                        for c, n in enumerate(out_of(h)):
                            split_head(tt["o", h] + c, ht_hi, h if heads == H1 else None, n)

            softmax_attention(ATT2_ORDER, TT2, H1, T, lambda h: (p2a, p2b)[h % 2], pt2, SC1, 0, lambda h: [CC + h // 2])
            for c in range(CC):
                act.wait_ge(ln_d, c + 1)
                if c >= 2:
                    act.wait_ge(ln_used, c - 1)
                st.done(act.activation(lnq[:, c % 2], ay[:, c], ACT.Square), ln_sq)
            t = Tile(T0["ln"] + 1)
            t.wait_full(act)
            st.done(act.activation(lnt[:], t.ap[:], ACT.Sqrt, bias=eps_t[:, 0:1], scale=1.0 / (CC * P)), tile=t)
            for c in range(CC):
                act.wait_ge(ln_y, c + 1)
                st.done(act.activation(ay[:, c], ay[:, c], ACT.Silu))
                st.after()
                st.done(act.copy(ht_hi[:, c], ay[:, c]), part_hi)
            post_and_norm(2, lambda m: post_psum(m, T0["w_out2"]), "nt4", ht_hi)
            for m in range(DC):
                copy_out(T0["mem_q"] + m, qm[:, m])
            softmax_attention(ATTM_ORDER, TTM, MH, NM, lambda h: pm[:, h % 2], ptm, SCM, NT * H1,
                              lambda h: [2 * h, 2 * h + 1])
            post_and_norm(3, lambda m: post_psum(m, T0["mem_o"]), "nt5", ht_hi)

            def ffn_up(t0, j, p, i=None):
                act.wait_ge(par_ready, j + 1)
                for c in range(4):
                    t = Tile(t0 + c, i, 24)
                    t.wait_full(act)
                    if c == 0 and (i is not None or j):
                        act.wait_ge(ffn_lo, j * 2)
                    g, k = c // 2, c % 2
                    st.done(act.activation(uc[:, c], t.ap[:], ACT.Identity, scale=par[:, p, 2 + g, k:k + 1],
                                           bias=par[:, p, 6 + g, k:k + 1]), uc_ready)
                for c in range(2):
                    Tile(t0 + c, i, 24).wait_taken(act)
                    st.done(act.activation(gact[:, c], uc[:, c], ACT.Gelu_apprx_tanh), gact_ready)
                for c in range(2):
                    act.wait_ge(gu_ready, j * 2 + c + 1)
                    st.done(act.copy(hf_hi[:, p, c], uc[:, 2 + c]), ffn_hi)

            t0 = T0["ffn"]
            ffn_up(t0, 0, 0)
            with st.loop((FF2_J - 1) // 2, {"uc_ready": 8, "gact_ready": 4, "ffn_hi": 4}) as i:
                ffn_up(t0 + 4, i * 2 + 1, 1, i)
                ffn_up(t0 + 16, i * 2 + 2, 0, i)
            last = t0 + 4 + 24 * ((FF2_J - 1) // 2)
            for m in range(NT):
                post_sbuf(facc2, m, (last + 2 * m, last + 2 * m + 1))

        @block.vector
        def _(v):
            st = Steps(v, dve_step)

            def do(ins, sem=None, tile=None):
                st.done(ins, sem, tile)

            def tt(o, a, b, op, sem=None, tile=None):
                st.after()
                do(v.tensor_tensor(o, a, b, op), sem, tile)

            def stt(o, a, s, b, op0, op1, sem=None, tile=None):
                st.after()
                do(v.scalar_tensor_tensor(out=o, in0=a, scalar=s, in1=b, op0=op0, op1=op1), sem, tile)

            def ts(o, a, s1, s2, op0, op1=ALU.bypass, sem=None, tile=None):
                st.after()
                if s2 is None:
                    do(v.tensor_scalar(o, a, s1, None, op0), sem, tile)
                else:
                    do(v.tensor_scalar(o, a, s1, s2, op0, op1), sem, tile)

            def recip(o, a, sem=None):
                st.after()
                do(v.reciprocal(o, a), sem)

            def col(n, k=1):
                return vec[:, n:n + k]

            def norm_inv_of(name, m):
                v.wait_ge(norm_std, NB[name] + m + 1)
                recip(stat[:, 16 + m:17 + m], stat[:, 8 + m:9 + m], norm_inv)

            def norm_turned(name, m, gain, hi, lo, shift=None, between=lambda: None):
                nb = NB[name] + m
                tv = [tmp[:, h].rearrange("p (c t) -> p c t", c=4) for h in range(2)]

                def wide(a, h):
                    return a[:, 4 * h:4 * h + 4].unsqueeze(2).broadcast_to([P, 4, P])
                for h in range(2):
                    t = Tile(turned(name, m, h))
                    t.wait_full(v)
                    tt(tv[h], t.ap[:].rearrange("p (c t) -> p c t", c=4), wide(gain, h), ALU.mult, tile=t)
                    if shift is not None:
                        tt(tv[h], tv[h], wide(shift, h), ALU.add, nt_tmp)
                    if h == (shift is None):
                        between()
                for h in range(2):
                    v.wait_ge(nt_hi, 2 * nb + h + 1)
                    sl = (slice(None), slice(4 * h, 4 * h + 4), slice(m * P, m * P + P))
                    tt(lo[sl], tv[h], hi[sl].bitcast(F32), ALU.subtract, nt_lo)

            def post(u, m, src, scaled, tiles=(None, None), add=True):
                v.wait_ge(post_std, NT * u + m + 1)
                recip(stat[:, 56 + m:57 + m], stat[:, 48 + m:49 + m])
                if u >= 2 and m == 0:
                    v.wait_ge(gp_loaded[u], 16)
                for h in range(2):
                    hc = slice(512 * h, 512 * h + 512)
                    stt(scaled[:, hc], src(h), stat[:, 56 + m:57 + m], gpost[:, u % 2, hc], ALU.mult, ALU.mult,
                        tile=tiles[h], sem=None if add or not h else ffn_scaled)
                for h in range(2 if add else 0):
                    hc = slice(512 * h, 512 * h + 512)
                    tt(x[:, m, hc], x[:, m, hc], scaled[:, hc], ALU.add, x_new if h else None)

            def post_psum(u, m, t0, name):
                if m >= 2:
                    Tile(turned(name, m - 2, 1)).wait_full(v)
                tiles = [Tile(t0 + 4 * h + m) for h in range(2)]
                post(u, m, lambda h: tiles[h].ap[:], xn[:, m % 2], tiles)

            def post_sbuf(u, m, src, add=True):
                post(u, m, lambda h: src[:, m, 512 * h:512 * h + 512], src[:, m], add=add)

            def post_and_norm(post_row, name, gain, hi, lo, shift=None):
                for m in range(NT + 1):
                    if m < NT:
                        post_row(m)
                    inv = (lambda: norm_inv_of(name, m)) if m < NT else (lambda: None)
                    if m:
                        norm_turned(name, m - 1, gain, hi, lo, shift, inv)
                    else:
                        inv()

            t = Tile(T0["vec"])
            t.wait_full(v)
            do(v.tensor_copy(vec[:], t.ap[:, 0:V_ALL]), tile=t)
            def ada_products(s):
                for c in range(DC):
                    i = DC * s + c
                    v.wait_ge(ada_loaded[i % 4], 16 * (i // 4 + 1))
                    if c == 0:
                        ts(ada_acc[:, s % 4], ada_w[:, i % 4], col(V_C), None, ALU.mult, sem=ada_used)
                    else:
                        stt(ada_acc[:, s % 4], ada_w[:, i % 4], col(V_C + c), ada_acc[:, s % 4],
                            ALU.mult, ALU.add, ada_used)

            def ada_finish(s):
                for h in range(2 if s in (2, 5) else 1):
                    t = Tile(ADA_T[s] + h)
                    t.wait_full(v)
                    if s in (2, 5):
                        j = s // 5
                        hc = slice(512 * h, 512 * h + 512)
                        if h == 0:
                            v.wait_ge(ada_b_loaded[j], 16)
                            v.wait_ge(gp_loaded[j], 16)
                        tt(tmp[:, h], t.ap[:], ada_b[:, hc], ALU.add, tile=t)
                        tt(gpost[:, j, hc], gpost[:, j, hc], tmp[:, h], ALU.mult, gp_made)
                    else:
                        j = {0: 0, 1: 1, 3: 2, 4: 3}[s]
                        tt(mod[:, j], t.ap[:, 0:DC], col(V_BADA + 8 * s, 8), ALU.add, tile=t)
                        if j % 2:
                            stt(mod[:, j], mod[:, j], 1.0, col((V_G1, V_GM1)[j // 2], 8), ALU.add, ALU.mult)

            ada_products(0)
            ada_products(1)
            ada_finish(0)
            ada_finish(1)
            for m in range(NT + 1):
                if m < NT:
                    norm_inv_of("nt1", m)
                if m:
                    norm_turned("nt1", m - 1, mod[:, 1], ht_hi, ht_lo, mod[:, 0])
            ada_products(2)
            ada_products(3)

            t0 = T0["w_in"]
            for m in range(CC):
                Tile(t0 + m).wait_taken(v)
                t = Tile(t0 + 4 + m)
                t.wait_full(v)
                tt(cv[:, m], t.ap[:], cv[:, m], ALU.mult, tile=t)
                w = [col(V_CW + 4 * k + m) for k in range(3)]
                ts(cy[:, m], cv[:, m], w[2], None, ALU.mult)
                stt(cy[:, m, 1:T], cv[:, m, 0:T - 1], w[1], cy[:, m, 1:T], ALU.mult, ALU.add)
                stt(cy[:, m, 2:T], cv[:, m, 0:T - 2], w[0], cy[:, m, 2:T], ALU.mult, ALU.add)
            ada_products(4)
            for m in range(CC):
                t = Tile(t0 + 8 + m)
                t.wait_full(v)
                tt(cy[:, m], t.ap[:], cy[:, m], ALU.mult, tile=t)
            for m in range(CC):
                v.wait_ge(part_hi, m + 1)
                tt(yt_lo[:, m], cy[:, m], yt_hi[:, m].bitcast(F32), ALU.subtract, part_lo)
            ada_products(5)
            for s in range(2, 6):
                ada_finish(s)

            def lo_of_head(t, hi, lo, h, n, seen):
                t = Tile(t)
                v.wait_ge(o_hi, seen)
                a, b = (0, P) if h is None else (HD * (h % 2), HD * (h % 2) + HD)
                tt(lo[a:b, n], t.ap[a:b, :], hi[a:b, n].bitcast(F32), ALU.subtract, tile=t)

            for qt in range(NT):
                st.after()
                do(v.memset(m1[:, O1[qt] + W1[qt]:O1[qt] + W1[qt] + 1], 1.0))
            for what, h in ATT1_ORDER:
                if what == "g" and h < 4:
                    for j in range(2):
                        Tile(TT["g", h] + j).wait_taken(v)
                        n = 2 * h + j
                        tt(mg[:, n], mg[:, n], tmp[:, n % 2], ALU.mult, gate_used)
                elif what == "z":
                    for qt in range(NT):
                        Tile(TT["z", h] + qt).wait_taken(v)
                        a, w = O1[qt], W1[qt]
                        d = slice(a + w - P, a + w)
                        tt(m1[:, d], m1[:, d], not_before[:], ALU.max)
                        tt(b1[:, h % 2, d], b1[:, h % 2, d], before[:], ALU.mult)
                        mr = m1[:, a + w:a:-1]
                        st.after()
                        do(v.tensor_tensor_scan(p1[:, w - 1::-1] if w == T else p1[:, w - 1::-1], mr, mr, 1.0,
                                                ALU.mult, ALU.bypass))
                        tt(b1[:, h % 2, a:a + w], b1[:, h % 2, a:a + w], p1[:, 0:w], ALU.mult, a1_ready)
                elif what == "o":
                    lo_of_head(TT["o", h], yt_hi, yt_lo, h, h // 2, h + 1)
            for m in range(DC + 1):
                if m < DC:
                    t = Tile(T0["pattn"] + m)
                    t.wait_full(v)
                    tt(sgb[:, m], t.ap[:], sgb[:, m], ALU.mult, tile=t)
                    tt(mg[:, m], mg[:, m], sgb[:, m], ALU.add, part_f32)
                if m:
                    v.wait_ge(part_hi, CC + m)
                    tt(ht_lo[:, m - 1], mg[:, m - 1], ht_hi[:, m - 1].bitcast(F32), ALU.subtract, part_lo)
            post_and_norm(lambda m: post_psum(0, m, T0["w_out"], "nt2"), "nt2", mod[:, 3], ht_hi, ht_lo, mod[:, 2])

            st.after()
            do(v.memset(facc[:], 0.0))
            st.after()

            def mlp_sum(m, h, t0, i=None):
                t = Tile(t0 + 8 + 4 * h + m, i, 16)
                t.wait_full(v)
                hc = slice(512 * h, 512 * h + 512)
                tt(facc[:, m, hc], t.ap[:], facc[:, m, hc], ALU.add, tile=t)

            def square_quarter(q, t0, i=None):
                for m in range(DC + 1):
                    if m < DC:
                        Tile(t0 + m, i, 16).wait_taken(v)
                        tt(tmp[:, m % 2], hr[:, m % 2], hr[:, m % 2], ALU.mult, part_f32)
                    if m:
                        v.wait_ge(part_hi, q * DC + CC + DC + m)
                        tt(hq_lo[:, m - 1], tmp[:, (m - 1) % 2], hq_hi[:, m - 1].bitcast(F32), ALU.subtract, part_lo)

            with st.loop(FF1_Q - 1, {"part_f32": DC, "part_lo": DC}) as i:
                square_quarter(i, T0["mlp"], i)
                for h in range(2):
                    for m in range(NT):
                        mlp_sum(m, h, T0["mlp"], i)
            last = T0["mlp"] + 16 * (FF1_Q - 1)
            square_quarter(FF1_Q - 1, last)

            def last_sum_and_post(m):
                for n in (0, 1) if m == 0 else (m + 1,) if m + 1 < NT else ():
                    mlp_sum(n, 0, last)
                    mlp_sum(n, 1, last)
                post_sbuf(1, m, facc)

            post_and_norm(last_sum_and_post, "nt3", col(V_NMIX, 8), ht_hi, ht_lo)

            norm_inv_of("memnt", 0)
            norm_inv_of("memnt", 1)
            st.after()
            do(v.memset(av[:, :, 0:pad], 0.0))
            st.after()
            do(v.memset(av[:, :, pad + T:], 0.0))
            t0 = T0["w_in2a"]
            for m in range(CC):
                Tile(t0 + m).wait_taken(v)
                Tile(t0 + 4 + m).wait_taken(v)
                tt(av[:, m, pad:pad + T], av[:, m, pad:pad + T], tmp[:, m % 2], ALU.mult, gate_used)
            for m in range(MT):
                norm_turned("memnt", m, col(V_MEMG, 8), mt_hi, mt_lo)
            v.wait_ge(tables_loaded, 16 * (2 + H1 + KV2))
            NQ = H1 + KV2
            for m in range(NT):
                Tile(T0["w_in2"] + m).wait_taken(v)
                v.wait_ge(k_in, m + 1)
                xq = qki[:, m]
                tt(qk_t[:], xq, xq, ALU.mult)
                st.after()
                do(v.tensor_reduce(qks[:, 0], qk_t[:], AX_X, ALU.add), rope_ss)
                v.wait_ge(rope_std, m + 1)
                recip(qks[:, 2], qks[:, 1])
                tt(xq, xq, qks[:, 2].unsqueeze(2).broadcast_to([P, NQ, HD]), ALU.mult)
                tt(xq, xq, qkg[:], ALU.mult)
                if m:
                    Tile(TT2["r", m - 1] + 1).wait_full(v)
                tt(qk[:], xq, rope[:, 0, m].unsqueeze(1).broadcast_to([P, NQ, HD]), ALU.mult)
                five = "p h (g s e) -> p h g s e"
                xi = xq.rearrange(five, g=2, s=2)
                xo = qk_t[:].rearrange(five, g=2, s=2)
                sn = rope[:, 1, m].rearrange("p (g s e) -> p g s e", g=2, s=2)
                for s in range(2):
                    tt(xo[:, :, :, s], xi[:, :, :, 1 - s],
                       sn[:, :, s].unsqueeze(1).broadcast_to([P, NQ, 2, HD // 4]), ALU.mult)
                tt(qk[:], qk[:], qk_t[:], ALU.add)
                st.after()
                do(v.tensor_copy(kd[:], qk[:, H1:].unsqueeze(2).broadcast_to([P, KV2, 2, HD])), qk_ready)

            def conv31():
                for c in range(CC - POOL_CC):
                    for k in range(K2):
                        w = col(V_CDW + CC * k + c)
                        if k == 0:
                            ts(ay[:, c], av[:, c, 0:T], w, col(V_CB + c), ALU.mult, ALU.add)
                        else:
                            stt(ay[:, c], av[:, c, k:k + T], w, ay[:, c], ALU.mult, ALU.add,
                                ay_ready if k == K2 - 1 else None)
                        yield

            taps = conv31()
            per_tile = -(-(CC - POOL_CC) * K2 // (H1 * NT))

            def softmax_attention(order, tiles, heads, keys, p_of, scale, mb, ob, out_of, fill):
                seen = ob
                for what, h in order:
                    if what == "z":
                        for qt in range(NT):
                            t = Tile(tiles["z", h] + qt)
                            t.wait_full(v)
                            st.after()
                            do(v.tensor_reduce(smx[:, 3, h % 2, qt:qt + 1], t.ap[:, 0:keys], AX_X, ALU.max))
                            ts(smx[:, 0, h % 2, qt:qt + 1], smx[:, 3, h % 2, qt:qt + 1], -scale, None, ALU.mult,
                               sem=sm_max)
                        for qt in range(NT):
                            fill()
                            Tile(tiles["z", h] + qt).wait_taken(v)
                            recip(smx[:, 2, h % 2, qt:qt + 1], smx[:, 1, h % 2, qt:qt + 1])
                            ts(p_of(h)[:, qt], p_of(h)[:, qt], smx[:, 2, h % 2, qt:qt + 1], None, ALU.mult, sem=sm_p)
                    elif what == "o":
                        for c, n in enumerate(out_of(h)):
                            seen += 1
                            lo_of_head(tiles["o", h] + c, ht_hi, ht_lo, h if heads == H1 else None, n, seen)

            softmax_attention(ATT2_ORDER, TT2, H1, T, lambda h: (p2a, p2b)[h % 2], SC1, 0, H1, lambda h: [CC + h // 2],
                              lambda: [next(taps, None) for _ in range(per_tile)])
            for _ in taps:
                pass
            t = Tile(T0["ln"])
            t.wait_full(v)
            ts(lnt[:], t.ap[:], 1.0 / (CC * P), None, ALU.mult, tile=t)
            for c in range(CC):
                tt(ay[:, c], ay[:, c], lnt[:], ALU.subtract, ln_d)
            Tile(T0["ln"] + 1).wait_taken(v)
            recip(lnt[:], lnt[:])
            for c in range(CC):
                tt(ay[:, c], ay[:, c], lnt[:], ALU.mult)
                ts(ay[:, c], ay[:, c], col(V_LNG + c), col(V_LNB + c), ALU.mult, ALU.add, sem=ln_y)
            for c in range(CC):
                v.wait_ge(part_hi, CC + DC + DC * FF1_Q + c + 1)
                tt(ht_lo[:, c], ay[:, c], ht_hi[:, c].bitcast(F32), ALU.subtract, part_lo)
            post_and_norm(lambda m: post_psum(2, m, T0["w_out2"], "nt4"), "nt4", col(V_NMEM, 8), ht_hi, ht_lo)
            softmax_attention(ATTM_ORDER, TTM, MH, NM, lambda h: pm[:, h % 2], SCM, NT * H1, 2 * H1,
                              lambda h: [2 * h, 2 * h + 1], lambda: None)
            post_and_norm(lambda m: post_psum(3, m, T0["mem_o"], "nt5"), "nt5", col(V_NFFN, 8), ht_hi, ht_lo)

            taps_v = vec[:, V_FFN:V_ALL].rearrange("p (k c) -> p k c", k=8)

            def ffn_up(t0, j, p, i=None):
                cols = slice(2 * j, 2 * j + 2) if i is None else bass.ds(j * 2, 2)
                st.after()
                if i is not None:
                    v.sem_inc(par_go, 1)
                do(v.tensor_copy(par[:, p], taps_v[:, :, cols]), par_ready)
                for c in range(4):
                    t = Tile(t0 + c, i, 24)
                    v.wait_ge(uc_ready, j * 4 + c + 1)
                    g, k = c // 2, c % 2
                    stt(uc[:, c, 1:T], t.ap[:, 0:T - 1], par[:, p, g, k:k + 1], uc[:, c, 1:T], ALU.mult, ALU.add)
                    stt(uc[:, c, 0:T - 1], t.ap[:, 1:T], par[:, p, 4 + g, k:k + 1], uc[:, c, 0:T - 1],
                        ALU.mult, ALU.add, tile=t)
                for c in range(2):
                    v.wait_ge(gact_ready, j * 2 + c + 1)
                    tt(uc[:, 2 + c], uc[:, 2 + c], gact[:, c], ALU.mult, gu_ready)
                for c in range(2):
                    v.wait_ge(ffn_hi, j * 2 + c + 1)
                    tt(hf_lo[:, p, c], uc[:, 2 + c], hf_hi[:, p, c].bitcast(F32), ALU.subtract, ffn_lo)

            def ffn_sum(m, t0, i=None):
                for h in range(2):
                    t = Tile(t0 + 2 * m + h, i, 24)
                    t.wait_full(v)
                    hc = slice(512 * h, 512 * h + 512)
                    tt(facc2[:, m, hc], t.ap[:], facc2[:, m, hc], ALU.add, tile=t)

            def ffn_down(t0, i=None):
                for m in range(NT):
                    ffn_sum(m, t0, i)

            st.after()
            do(v.memset(facc2[:], 0.0))
            st.after()
            t0 = T0["ffn"]
            ffn_up(t0, 0, 0)
            with st.loop((FF2_J - 1) // 2, {"par_ready": 2, "dve_step": 8, "gu_ready": 4, "ffn_lo": 4}) as i:
                ffn_up(t0 + 4, i * 2 + 1, 1, i)
                ffn_down(t0 + 8, i)
                ffn_up(t0 + 16, i * 2 + 2, 0, i)
                ffn_down(t0 + 20, i)
            for m in range(NT):
                ffn_sum(m, t0 + 4 + 24 * ((FF2_J - 1) // 2))
                post_sbuf(4, m, facc2, add=m == NT - 1)


FLAT = ("c", "b_ada", "g_pre_mix", "g_post_mix", "g_pre_mlp", "g_post_mlp", "conv_w", "norm_mix_pre_2", "conv_dw_2",
        "conv_dw_b_2", "conv_ln_g_2", "conv_ln_b_2", "q_norm_g_2", "k_norm_g_2", "norm_mix_post_2", "norm_mem_pre_2",
        "mem_norm_g_2", "norm_mem_post_2", "norm_ffn_pre_2", "ffn_dw_2", "ffn_dw_b_2", "norm_ffn_post_2")
MATS = ("x", "w_ada", "w_in", "w_proj_conv", "w_proj_attn", "w_out", "w_mlp_in", "w_mlp_out", "mem_2", "w_in_2",
        "w_out_2", "w_mem_q_2", "w_mem_kv_2", "w_mem_o_2", "w_up_2", "w_down_2")


def rope_tables():
    grid_w, axis = 64, HD // 2
    inv = (np.float32(10000.0) ** (-np.arange(0, axis, 2, dtype=np.float32) / np.float32(axis))).astype(np.float32)
    tok = np.arange(T)
    ang = [(p.astype(np.float32)[:, None] * inv[None, :]) for p in (tok // grid_w, tok % grid_w)]
    cos = np.concatenate([f(a) for a in ang for f in (np.cos, np.cos)], axis=1)
    sin = np.concatenate([s * np.sin(a) for a in ang for s in (-1, 1)], axis=1)
    return cos.astype(np.float32), sin.astype(np.float32)


def kernel(**inputs):
    import concourse.bacc as bacc
    from concourse.bass_utils import run_bass_kernel_spmd

    nc = bacc.Bacc("TRN2", target_bir_lowering=False, num_devices=1)
    arrays = {name: np.ascontiguousarray(inputs[name]).reshape(-1) for name in FLAT}
    for name in MATS:
        a = np.ascontiguousarray(inputs[name])
        arrays[name] = a.reshape(a.shape[-2:])
    arrays["rope_cos"], arrays["rope_sin"] = rope_tables()
    A = {name: nc.dram_tensor("in_" + name, a.shape, F32, kind="ExternalInput").ap() for name, a in arrays.items()}
    out = nc.dram_tensor("out", (T, D), F32, kind="ExternalOutput").ap()
    build(nc, A, out)
    r = run_bass_kernel_spmd(nc, [{"in_" + name: a for name, a in arrays.items()}], core_ids=[0])
    return r.results[0]["out"].reshape(1, T, D)
```
